# Optimizing a Trainium2 kernel written in Bass

```python
import math
import jax, jax.numpy as jnp
from jax import lax
import numpy as np

D_MODEL = 1024
BATCH = 1
SEQ = 2048
DEPTH = 1

MEM_LEN = 256
SB_HEADS = 4
SB_HEAD_DIM = 128
SB_WIDTH = SB_HEADS * SB_HEAD_DIM
Q_BLOCK = 128
POOL_WINDOWS = (2, 4, 8, 16)
POOL_GROUPS = 4
POOL_GROUP_DIM = 128
POOL_WIDTH = POOL_GROUPS * POOL_GROUP_DIM
LRU_BLOCKS = 8
LRU_BLOCK_DIM = 64
LRU_WIDTH = LRU_BLOCKS * LRU_BLOCK_DIM
CONV_WIDTH = 4
LRU_C = 8.0
XA_HEADS = 4
XA_HEAD_DIM = 128
XA_WIDTH = XA_HEADS * XA_HEAD_DIM
N_BRANCH = 4
BRANCH_WIDTH = 512
DN_ALPHA = (2 * DEPTH) ** 0.25
DN_BETA = (8 * DEPTH) ** -0.25
LN_EPS = 1e-5
SPLIT_SIZES = (SB_WIDTH, SB_WIDTH, SB_WIDTH, SB_WIDTH, POOL_WIDTH, POOL_WIDTH, LRU_WIDTH, LRU_WIDTH, XA_WIDTH, XA_WIDTH, N_BRANCH * D_MODEL)
IN_WIDTH = 10 * 512 + N_BRANCH * D_MODEL

kernel_name = 'hybrid_stickbreak_pool_rglru_memxattn'

def _split_columns(p):
    out, off = [], 0
    for size in SPLIT_SIZES:
        out.append(p[..., off:off + size])
        off += size
    return out

def layer_norm(x, g, b):
    xf = x.astype(jnp.float32)
    mean = jnp.mean(xf, axis=-1, keepdims=True)
    var = jnp.mean(jnp.square(xf - mean), axis=-1, keepdims=True)
    y = (xf - mean) * lax.rsqrt(var + LN_EPS) * g.astype(jnp.float32) + b.astype(jnp.float32)
    return y.astype(x.dtype)

def stick_breaking_attention(q, k, v):
    b, s, h, d = q.shape
    nb = s // Q_BLOCK
    scale = 1.0 / math.sqrt(d)
    qh = q.transpose(0, 2, 1, 3)
    kh = k.transpose(0, 2, 1, 3).reshape(b, h, nb, Q_BLOCK, d)
    vh = v.transpose(0, 2, 1, 3).reshape(b, h, nb, Q_BLOCK, d)
    loc = jnp.arange(Q_BLOCK)
    suffix = (loc[:, None] > loc[None, :]).astype(jnp.float32)
    diag_valid = loc[None, :] < loc[:, None]
    outs = []
    for i in range(nb):
        nk = i + 1
        q_blk = qh[:, :, i * Q_BLOCK:(i + 1) * Q_BLOCK]
        k_pre = kh[:, :, :nk]
        v_pre = vh[:, :, :nk]
        z = jnp.einsum('bhqd,bhnkd->bhqnk', q_blk, k_pre, preferred_element_type=jnp.float32) * scale
        blk_idx = jnp.arange(nk)
        valid = (blk_idx[None, :, None] < i) | diag_valid[:, None, :]
        log_1m = jnp.where(valid, jax.nn.log_sigmoid(-z), 0.0)
        within = jnp.einsum('bhqnk,kj->bhqnj', log_1m, suffix)
        totals = jnp.sum(log_1m, axis=-1)
        later = lax.cumsum(totals, axis=3, reverse=True) - totals
        w = jnp.where(valid, jnp.exp(jax.nn.log_sigmoid(z) + within + later[..., None]), 0.0)
        o = jnp.einsum('bhqnk,bhnkd->bhqd', w.astype(v.dtype), v_pre, preferred_element_type=jnp.float32)
        outs.append(o.astype(v.dtype))
    out = jnp.concatenate(outs, axis=2)
    return out.transpose(0, 2, 1, 3).reshape(b, s, h * d)

def multiscale_pool(u, w_pool, pool_scale):
    b, s, c = u.shape
    uf = u.astype(jnp.float32)
    csum = jnp.concatenate([jnp.zeros((b, 1, c), jnp.float32), jnp.cumsum(uf, axis=1)], axis=1)
    pos = jnp.arange(s)
    groups = []
    for g, win in enumerate(POOL_WINDOWS):
        sl = slice(g * POOL_GROUP_DIM, (g + 1) * POOL_GROUP_DIM)
        start = jnp.maximum(pos + 1 - win, 0)
        window_sum = csum[:, 1:, sl] - csum[:, start, sl]
        count = (pos + 1 - start).astype(jnp.float32)[None, :, None]
        groups.append(window_sum / count - uf[:, :, sl])
    pooled = jnp.stack(groups, axis=2)
    mixed = jnp.einsum('bsgi,gij->bsgj', pooled, w_pool.astype(jnp.float32)).reshape(b, s, c)
    return (mixed * pool_scale.astype(jnp.float32)).astype(u.dtype)

def rg_lru(u, conv_w, conv_b, w_rg, b_rg, w_ig, b_ig, lru_L):
    b, s, c = u.shape
    xc = lax.conv_general_dilated(u, conv_w[:, None, :], window_strides=(1,), padding=[(CONV_WIDTH - 1, 0)],
                                  dimension_numbers=('NWC', 'WIO', 'NWC'), feature_group_count=c) + conv_b
    xb = xc.reshape(b, s, LRU_BLOCKS, LRU_BLOCK_DIM)
    r = jax.nn.sigmoid(jnp.einsum('bshi,hij->bshj', xb, w_rg).reshape(b, s, c) + b_rg)
    i = jax.nn.sigmoid(jnp.einsum('bshi,hij->bshj', xb, w_ig).reshape(b, s, c) + b_ig)
    log_a = (-LRU_C * r.astype(jnp.float32)) * jax.nn.softplus(-lru_L.astype(jnp.float32))
    a = jnp.exp(log_a)
    mult = jnp.sqrt(-jnp.expm1(2.0 * log_a))
    bx = mult * (i * xc).astype(jnp.float32)

    def combine(left, right):
        a_l, b_l = left
        a_r, b_r = right
        return a_l * a_r, a_r * b_l + b_r

    _, h = lax.associative_scan(combine, (a, bx), axis=1)
    return h.astype(u.dtype)

def memory_cross_attention(q, mem, w_mem_kv):
    b, s, _ = q.shape
    m = mem.shape[1]
    kv = mem @ w_mem_kv
    k = kv[..., :XA_WIDTH].reshape(b, m, XA_HEADS, XA_HEAD_DIM)
    v = kv[..., XA_WIDTH:].reshape(b, m, XA_HEADS, XA_HEAD_DIM)
    qh = q.reshape(b, s, XA_HEADS, XA_HEAD_DIM)
    scores = jnp.einsum('bshd,bmhd->bhsm', qh, k, preferred_element_type=jnp.float32) / math.sqrt(XA_HEAD_DIM)
    p = jax.nn.softmax(scores, axis=-1)
    out = jnp.einsum('bhsm,bmhd->bshd', p.astype(v.dtype), v)
    return out.reshape(b, s, XA_WIDTH)

def hybrid_layer(x, mem, w_in, w_pool, pool_scale, conv_w, conv_b, w_rg, b_rg, w_ig, b_ig, lru_L,
                 w_mem_kv, w_branch, w_out, ln_g, ln_b):
    b, s, d = x.shape
    proj = x @ w_in
    (q_sb, k_sb, v_sb, g_sb, u_pool, g_pool, u_lru, g_lru, q_xa, g_xa, merge) = _split_columns(proj)
    hs = (b, s, SB_HEADS, SB_HEAD_DIM)
    y_sb = stick_breaking_attention(q_sb.reshape(hs), k_sb.reshape(hs), v_sb.reshape(hs)) * jax.nn.silu(g_sb)
    y_pool = multiscale_pool(u_pool, w_pool, pool_scale) * jax.nn.silu(g_pool)
    y_lru = rg_lru(u_lru, conv_w, conv_b, w_rg, b_rg, w_ig, b_ig, lru_L) * jax.nn.silu(g_lru)
    y_xa = memory_cross_attention(q_xa, mem, w_mem_kv) * jax.nn.silu(g_xa)
    gates = jax.nn.sigmoid(merge.reshape(b, s, N_BRANCH, d))
    branches = (y_sb, y_pool, y_lru, y_xa)
    merged = gates[:, :, 0] * (branches[0] @ w_branch[0])
    for n in range(1, N_BRANCH):
        merged = merged + gates[:, :, n] * (branches[n] @ w_branch[n])
    out = merged @ w_out
    return layer_norm(DN_ALPHA * x + out, ln_g, ln_b)

def setup_inputs(seed: int = 0) -> dict:
    key = jax.random.key(seed)
    ks = jax.random.split(key, 20)
    f32 = jnp.float32
    nrm = lambda k, shape, fan_in, mult=1.0: jax.random.normal(k, shape, f32) * (fan_in ** -0.5) * mult
    x = jax.random.normal(ks[0], (BATCH, SEQ, D_MODEL), f32)
    mem = jax.random.normal(ks[1], (BATCH, MEM_LEN, D_MODEL), f32)
    w_in = nrm(ks[2], (DEPTH, D_MODEL, IN_WIDTH), D_MODEL)
    w_pool = nrm(ks[3], (DEPTH, POOL_GROUPS, POOL_GROUP_DIM, POOL_GROUP_DIM), POOL_GROUP_DIM)
    pool_scale = 1.0 + 0.02 * jax.random.normal(ks[4], (DEPTH, POOL_WIDTH), f32)
    conv_w = nrm(ks[5], (DEPTH, CONV_WIDTH, LRU_WIDTH), CONV_WIDTH)
    conv_b = 0.01 * jax.random.normal(ks[6], (DEPTH, LRU_WIDTH), f32)
    w_rg = nrm(ks[7], (DEPTH, LRU_BLOCKS, LRU_BLOCK_DIM, LRU_BLOCK_DIM), LRU_BLOCK_DIM)
    b_rg = 0.01 * jax.random.normal(ks[8], (DEPTH, LRU_WIDTH), f32)
    w_ig = nrm(ks[9], (DEPTH, LRU_BLOCKS, LRU_BLOCK_DIM, LRU_BLOCK_DIM), LRU_BLOCK_DIM)
    b_ig = 0.01 * jax.random.normal(ks[10], (DEPTH, LRU_WIDTH), f32)
    a_c = jax.random.uniform(ks[11], (DEPTH, LRU_WIDTH), f32, minval=0.9, maxval=0.999)
    sig = a_c ** (1.0 / LRU_C)
    lru_L = jnp.log(sig) - jnp.log1p(-sig)
    w_mem_kv = nrm(ks[12], (DEPTH, D_MODEL, 2 * XA_WIDTH), D_MODEL)
    w_branch = nrm(ks[13], (DEPTH, N_BRANCH, BRANCH_WIDTH, D_MODEL), BRANCH_WIDTH, DN_BETA)
    w_out = nrm(ks[14], (DEPTH, D_MODEL, D_MODEL), D_MODEL, DN_BETA)
    ln_g = 1.0 + 0.02 * jax.random.normal(ks[15], (DEPTH, D_MODEL), f32)
    ln_b = 0.02 * jax.random.normal(ks[16], (DEPTH, D_MODEL), f32)
    return {'x': x, 'mem': mem, 'w_in': w_in, 'w_pool': w_pool, 'pool_scale': pool_scale,
            'conv_w': conv_w, 'conv_b': conv_b, 'w_rg': w_rg, 'b_rg': b_rg, 'w_ig': w_ig, 'b_ig': b_ig,
            'lru_L': lru_L, 'w_mem_kv': w_mem_kv, 'w_branch': w_branch, 'w_out': w_out,
            'ln_g': ln_g, 'ln_b': ln_b}

def reference(x, mem, w_in, w_pool, pool_scale, conv_w, conv_b, w_rg, b_rg, w_ig, b_ig, lru_L,
              w_mem_kv, w_branch, w_out, ln_g, ln_b):
    for l in range(DEPTH):
        x = hybrid_layer(x, mem, w_in[l], w_pool[l], pool_scale[l], conv_w[l], conv_b[l], w_rg[l], b_rg[l],
                         w_ig[l], b_ig[l], lru_L[l], w_mem_kv[l], w_branch[l], w_out[l], ln_g[l], ln_b[l])
    return x


_drawn_inputs = setup_inputs


def setup_inputs(seed=0):
    import zlib

    import numpy as np

    out = dict(_drawn_inputs(seed))
    spreads = {}
    factors = {'mem': 6.048,
     'pool_scale': 200.0,
     'conv_b': 200.0,
     'b_rg': 200.0,
     'b_ig': 200.0,
     'w_mem_kv': 5.701,
     'ln_g': 23.431,
     'ln_b': 23.421,
     'conv_w': 25.984,
     'w_rg': 64.0,
     'w_ig': 37.592,
     'lru_L': 44.536}
    for name, (base, spread) in spreads.items():
        noise = np.random.default_rng([zlib.crc32(name.encode()), seed]).standard_normal(out[name].shape)
        drawn = base * np.exp(spread * noise) if base else spread * noise
        out[name] = __import__('jax').numpy.asarray(drawn.astype(out[name].dtype))
    for name, factor in factors.items():
        out[name] = (out[name] * factor).astype(out[name].dtype)
    return out
```

```python
from contextlib import ExitStack

import concourse.bass as bass
from concourse import mybir

F32 = mybir.dt.float32
F32R = mybir.dt.float32r
ALU = mybir.AluOpType
ACT = mybir.ActivationFunctionType
AX_X = mybir.AxisListType.X

P = 128
SEQ = 2048
D = 1024
MEM = 256
HALVES = 2
T = SEQ // HALVES
C = 512
NC = T // C
KD = D // P
HEADS = 4
KB = HEADS
NB = 4
FT = D // P
TB = T // P
SCALE = float(P) ** -0.5
LN_EPS = 1e-5
LRU_C = 8.0
ALPHA = 2.0 ** 0.25
TAPS = 4
XP = 8
HALO = 16
WINDOWS = (2, 4, 8, 16)
ROOT_UP = 2.0 ** 100
ROOT_DOWN = 2.0 ** -50

SET_EXP_TANH, SET_SIGMOID, SET_SQRT, SET_EXP_LN = 0, 2, 3, 6

MEM_TILES = 2 * HEADS
PER_HALF = 4 * HEADS + 3 * 2 * HEADS + NB * FT + FT
C_ID, C_SUF, C_CAR, C_DIAG, C_CNT = 0, P, 2 * P, 3 * P, 4 * P
C_ALL = 4 * P + len(WINDOWS) * HALO
P_TAPS, P_CB, P_BR, P_BI, P_NSP, P_SCALE = 0, 4, 5, 6, 7, 8
P_ALL = 9

POOL_OUT = [(g + 1) % 2 for g in range(4)]

SUMS, USE, EARLY = 3, 4, 4


def wait_if(engine, semaphore, count):
    if not (isinstance(count, int) and count <= 0):
        engine.wait_ge(semaphore, count)


def each(engine, first_too, n, body):
    if first_too:
        body(0)
    with engine.Fori(1 if first_too else 0, n) as i:
        body(i)


def steps_of(half):
    out = []
    for c in range(NC):
        q0 = (half * NC + c) * (C // P)
        top = q0 + C // P - 1
        for b in range(top, -1, -1):
            out.append((c, b, P * max(b - q0, 0), b == top, b == 0, b >= q0))
    return out


def build(nc, xt, xrow, memt, w8, w4, wgate, wpool, prm, cst, ln_g, ln_b, out):
    with ExitStack() as ctx:
        base = (nc.sbuf_base + 31) // 32 * 32

        def at(name, offset, shape, dt=F32):
            return nc.alloc_sbuf_tensor_at(name, [P] + shape, dt, offset=base + offset)

        def sem(name):
            return ctx.enter_context(nc.semaphore(name))

        KIB = 1024
        XH = at("XH", 0, [KD, T], F32R)
        XL = at("XL", 32 * KIB, [KD, T], F32R)
        YH = at("YH", 64 * KIB, [KB, T], F32R)
        YL = at("YL", 80 * KIB, [KB, T], F32R)
        RAW = [at(f"RAW{i}", (96 + 4 * i) * KIB, [KD, P]) for i in range(2)]
        WH = [at(f"WH{i}", (104 + 4 * i) * KIB, [KD, P], F32R) for i in range(2)]
        WL = [at(f"WL{i}", (112 + 4 * i) * KIB, [KD, P], F32R) for i in range(2)]
        BRAW = [at(f"BRAW{i}", (120 + 2 * i) * KIB, [KB, P]) for i in range(2)]
        BH = [at(f"BH{i}", (124 + 2 * i) * KIB, [KB, P], F32R) for i in range(2)]
        BL = [at(f"BL{i}", (128 + 2 * i) * KIB, [KB, P], F32R) for i in range(2)]
        R1, R2, RC = 132 * KIB, 164 * KIB, 204 * KIB + 64
        IDENT = at("IDENT", RC, [P])
        SUFFIX = at("SUFFIX", RC + 512, [P], F32R)
        CARRY = at("CARRY", RC + 1024, [P], F32R)
        DIAG = at("DIAG", RC + 1536, [P])
        COUNT = at("COUNT", RC + 2048, [len(WINDOWS), HALO])
        PRM = at("PRM", RC + 2304, [KB, P_ALL])
        GP = at("GP", RC + 2464, [P_ALL])
        HSTATE = at("HSTATE", RC + 2528, [KB])
        LHALO = at("LHALO", RC + 2560, [KB, 4])
        PHALO = at("PHALO", RC + 2624, [KB, HALO])
        SM = at("SM", RC + 2880, [32])
        SM2 = at("SM2", RC + 3008, [64])
        STATS = at("STATS", RC + 3264, [TB, 12])

        MERGED = at("MERGED", R1, [FT, T])
        E = [at(f"E{i}", R1 + 2 * i * KIB if i < 2 else 126 * KIB, [C]) for i in range(3)]
        PF = [at(f"PF{i}", R1 + (4 + 2 * i) * KIB, [C]) for i in range(2)]
        PHI = [at(f"PHI{i}", R1 + (8 + 2 * i) * KIB if i < 3 else R2 + 36 * KIB, [C], F32R) for i in range(4)]
        PLO = [at(f"PLO{i}", R1 + (14 + 2 * i) * KIB if i < 3 else R2 + 38 * KIB, [C], F32R) for i in range(4)]
        ARG = [at(f"ARG{i}", R1 + (20 + 2 * i) * KIB, [C]) for i in range(4)]
        W = [at(f"W{i}", R1 + (28 + 2 * i) * KIB, [C]) for i in range(2)]
        VT = at("VT", R1 + 28 * KIB, [T])
        CRAW = at("CRAW", R1, [C_ALL])
        MRAW = at("MRAW", R1 + 4 * KIB, [KD, MEM])
        MTH = at("MTH", R1 + 12 * KIB, [KD, MEM], F32R)
        MTL = at("MTL", R1 + 20 * KIB, [KD, MEM], F32R)

        XRAW = at("XRAW", R2, [KD, T])
        QH = at("QH", R2, [T], F32R)
        QL = at("QL", R2 + 4 * KIB, [T], F32R)
        KH = at("KH", R2 + 8 * KIB, [SEQ], F32R)
        KL = at("KL", R2 + 16 * KIB, [SEQ], F32R)
        V = at("V", R2 + 24 * KIB, [SEQ // P, P])
        SG = at("SG", R2 + 32 * KIB, [T])
        GT = [at(f"GT{i}", R2 + (32 + 4 * i) * KIB, [T]) for i in range(2)]
        PU = at("PU", R2, [HALO + T])
        PS = [at(f"PS{i}", R2 + (i + 1) * (HALO + T) * 4, [HALO + T]) for i in range(2)]
        p0 = R2 + 3 * (HALO + T) * 4
        PLH = at("PLH", p0, [T], F32R)
        PLL = at("PLL", p0 + 4 * KIB, [T], F32R)
        PG = at("PG", p0 + 8 * KIB, [T])
        WPR = at("WPR", p0 + 12 * KIB, [HEADS, P])
        WPH = at("WPH", p0 + 14 * KIB, [HEADS, P], F32R)
        WPL = at("WPL", p0 + 16 * KIB, [HEADS, P], F32R)
        XC = [at(f"XC{i}", R2 + 4 * i * KIB, [T]) for i in range(2)]
        LI, LR, LA, LT, LG = (at(name, R2 + 4 * (i + 2) * KIB, [T])
                              for i, name in enumerate(("LI", "LR", "LA", "LT", "LG")))
        LU = at("LU", R2 + 28 * KIB, [4 + T])
        XCH = at("XCH", R2 + 32 * KIB + 32, [T], F32R)
        XCL = at("XCL", R2 + 36 * KIB + 32, [T], F32R)
        WGH = at("WGH", 124 * KIB, [2, P], F32R)
        WGR = at("WGR", 125 * KIB, [2, P])
        WGL = at("WGL", 128 * KIB, [2, P], F32R)
        NEVER = at("NEVER", 128 * KIB, [P])
        KMA = [at(f"KMA{i}", (64 + 4 * i) * KIB, [HEADS, MEM], F32R) for i in range(2)]
        VMA = at("VMA", 72 * KIB, [HEADS, MEM // P, P])
        KM = [at(f"KM{i}", R2 + (12 + i) * KIB, [MEM], F32R) for i in range(2)]
        VM = at("VM", R2 + 14 * KIB, [MEM // P, P])
        AG = at("AG", R2 + 8 * KIB, [T])
        PR = [at(f"PR{c}", R2 + (16 + 4 * c) * KIB, [C // P, MEM]) for c in range(NC)]
        PT = [at(f"PT{c}", R2 + (24 + 4 * c) * KIB, [MEM // P, C]) for c in range(NC)]
        MH = [at(f"MH{i}", (16 + 4 * i) * KIB, [KD, P], F32R) for i in range(2)]
        ML = [at(f"ML{i}", (24 + 4 * i) * KIB, [KD, P], F32R) for i in range(2)]
        LNG = at("LNG", 56 * KIB, [D])
        LNB = at("LNB", 60 * KIB, [D])
        WO = [[at("WO0H", R2, [KD, C], F32R), at("WO0L", R2 + 16 * KIB, [KD, C], F32R)],
              [at("WO1H", 0, [KD, C], F32R), at("WO1L", 32 * KIB, [KD, C], F32R)]]
        RES = [at(f"RES{t}", (64 + 4 * t) * KIB, [D]) for t in range(TB)]

        k_keep = nc.dram_tensor("k_keep", (HEADS, 2, P, T), F32).ap()
        v_keep = nc.dram_tensor("v_keep", (HEADS, P, TB * P), F32).ap()
        km_keep = nc.dram_tensor("km_keep", (HEADS, 2, P, MEM), F32).ap()
        vm_keep = nc.dram_tensor("vm_keep", (HEADS, P, MEM // P * P), F32).ap()

        def bank(name):
            return ctx.enter_context(nc.psum_tensor(name, [P, C], F32))

        PJ = [[bank(f"PJ{p}{c}") for c in range(NC)] for p in range(2)]
        Z = [bank(f"Z{i}") for i in range(2)]
        ACC = bank("ACC")
        OB = bank("OB")
        BR = [[Z[0], Z[1]], [ACC, OB]]
        ZB = [Z[0], Z[1], PJ[1][0], PJ[1][1]]
        TURNED = [PJ[0][0], PJ[1][0]]
        SUM = [ACC, PJ[0][1]]
        OUT = [PJ[0][0], OB]

        def z_bank(s):
            return OB if s == 2 else PJ[0][1] if s == 3 else ZB[s % 4]

        ROWS = PJ[0] + Z + PJ[1] + [ACC, OB]

        w_raw, w_hi, w_lo = [sem(f"w_raw{i}") for i in range(2)], sem("w_hi"), sem("w_lo")
        tile_done, pj_free = sem("tile_done"), sem("pj_free")
        b_raw, b_hi, b_lo = [sem(f"b_raw{i}") for i in range(2)], sem("b_hi"), sem("b_lo")
        branch_done = sem("branch_done")
        c_in, c_made, exp_l, small = sem("c_in"), sem("c_made"), sem("exp_l"), sem("small")
        m_in, m_hi, m_lo = [sem(f"m_in{i}") for i in range(2)], sem("m_hi"), sem("m_lo")
        mk_hi, mk_kept = sem("mk_hi"), sem("mk_kept")
        x_in, x_hi, x_lo = [sem(f"x_in{i}") for i in range(XP)], sem("x_hi"), sem("x_lo")
        q_hi, k_hi, v_tr, v_blk, sb_sig = sem("q_hi"), sem("k_hi"), sem("v_tr"), sem("v_blk"), sem("sb_sig")
        never_made, kv_back, kv_kept = sem("never_made"), sem("kv_back"), sem("kv_kept")
        z_done, abs_done, exp_done, ln_done = sem("z_done"), sem("abs_done"), sem("exp_done"), sem("ln_done")
        p_done, p_masked, p_hi, p_lo = sem("p_done"), sem("p_masked"), sem("p_hi"), sem("p_lo")
        m_done, m_masked, acc_done = sem("m_done"), sem("m_masked"), sem("acc_done")
        arg_done, w_done, pv_done = sem("arg_done"), sem("w_done"), sem("pv_done")
        y_f, y_hi, y_lo = sem("y_f"), sem("y_hi"), sem("y_lo")
        zeroed, gate_sig, merged = sem("zeroed"), sem("gate_sig"), sem("merged")
        pw_in, pw_hi, pw_lo = sem("pw_in"), sem("pw_hi"), sem("pw_lo")
        pl_f, pl_hi, pl_lo = sem("pl_f"), sem("pl_hi"), sem("pl_lo")
        p_sig, mix_done = sem("p_sig"), sem("mix_done")
        gw_in, gw_hi, gw_lo = sem("gw_in"), sem("gw_hi"), sem("gw_lo")
        xc_f, xc_hi, xc_lo = sem("xc_f"), sem("xc_hi"), sem("xc_lo")
        gates_done, l_act, l_var = sem("gates_done"), sem("l_act"), sem("l_var")
        km_back, vm_back, xq_hi, x_sig = sem("km_back"), sem("vm_back"), sem("xq_hi"), sem("x_sig")
        sc_done, xm_step, mx_done, ex_done = sem("sc_done"), sem("xm_step"), sem("mx_done"), sem("ex_done")
        nm_done, tr_done, pt_done, xo_done = sem("nm_done"), sem("tr_done"), sem("pt_done"), sem("xo_done")
        mt_hi, mt_lo, part_done, part_free = sem("mt_hi"), sem("mt_lo"), sem("part_done"), sem("part_free")
        xr_in, ln_in, stat_done = [sem(f"xr_in{i}") for i in range(TB)], sem("ln_in"), sem("stat_done")
        var_done, std_done, o_ready, o_out = sem("var_done"), sem("std_done"), sem("o_ready"), sem("o_out")

        STEPS = [steps_of(h) for h in range(HALVES)]
        NS = [len(s) for s in STEPS]
        ENDS = [[1 + max(i for i, step in enumerate(s) if step[0] == c) for c in range(NC)] for s in STEPS]
        ND = NC * (C // P)

        def first_tile(half, phase=0):
            return MEM_TILES + half * PER_HALF + phase

        M0 = 4 * HEADS
        POOL0 = M0 + FT
        M1 = POOL0 + 2 * HEADS
        LRU0 = M1 + FT
        M2 = LRU0 + 2 * HEADS
        XA0 = M2 + FT
        M3 = XA0 + 2 * HEADS
        WO0 = M3 + FT
        PIECES = [(0, 6), (6, KD)]
        SPLITS = 2 * TB + 1
        Y_HALF = NB * KB * NC

        block = ctx.enter_context(nc.Block())

        @block.sync
        def _(sp):
            def load_w8(half, k, p):
                sp.wait_ge(w_lo, first_tile(half, k) - 1)
                sp.dma_start(RAW[p][:], w8[bass.ds(MEM_TILES + k, 1)].rearrange("o p n -> (o p) n")
                             ).then_inc(w_raw[p], 16)

            sp.dma_start(MRAW[:, 0:KD // 2], memt[:, 0:KD // 2]).then_inc(m_in[0], 16)
            sp.dma_start(RAW[0][:], w8[0]).then_inc(w_raw[0], 16)
            sp.dma_start(MRAW[:, KD // 2:], memt[:, KD // 2:]).then_inc(m_in[1], 16)
            sp.dma_start(CRAW[:], cst).then_inc(c_in, 16)
            sp.dma_start(PRM[:], prm).then_inc(c_in, 16)

            def load_x(half, j):
                k = slice(j * KD // XP, (j + 1) * KD // XP)
                sp.dma_start(XRAW[:, k, :], xt[half, :, k, :]).then_inc(x_in[j], 16)

            for k in range(1, MEM_TILES):
                if k >= 2:
                    sp.wait_ge(w_lo, k - 1)
                sp.dma_start(RAW[k % 2][:], w8[k]).then_inc(w_raw[k % 2], 16)
                if k <= XP // 2:
                    load_x(0, 2 * k - 2)
                    load_x(0, 2 * k - 1)
            for half in range(HALVES):
                with sp.Fori(1 if half else 0, 2 * HEADS) as i:
                    for p in range(2):
                        load_w8(half, 2 * i + p, p)
                for n in range(NB):
                    at0 = (M0, M1, M2, M3)[n]

                    def pair_of_tiles(i, half=half):
                        for p in range(2):
                            load_w8(half, at0 + 2 * i + p, p)
                            f = 2 * i + p
                            wait_if(sp, b_lo, (half * NB + n) * FT + f - 1)
                            sp.dma_start(BRAW[p][:], w4[bass.ds(n * FT + f, 1)].rearrange("o p n -> (o p) n")
                                         ).then_inc(b_raw[p], 16)

                    each(sp, half == 0 and n == 0, FT // 2, pair_of_tiles)
                    if n < 3:
                        with sp.Fori(0, HEADS) as i:
                            for p in range(2):
                                load_w8(half, at0 + FT + 2 * i + p, p)
                for k in range(6):
                    load_w8(half, WO0 + k, k % 2)
                sp.wait_ge(y_lo, (half + 1) * Y_HALF)
                sp.wait_ge(branch_done, (half + 1) * NB * FT)
                for t in range(TB):
                    g = half * TB + t
                    sp.dma_start(RES[t][:], xrow[g * P:(g + 1) * P, :]).then_inc(xr_in[t], 16)
                sp.wait_ge(tile_done, first_tile(half, WO0))
                sp.dma_start(LNG[:], ln_g.rearrange("(o d) -> o d", o=1).partition_broadcast(P)).then_inc(ln_in, 16)
                sp.dma_start(LNB[:], ln_b.rearrange("(o d) -> o d", o=1).partition_broadcast(P)).then_inc(ln_in, 16)
                for k in range(6, FT):
                    load_w8(half, WO0 + k, k % 2)
                if half + 1 < HALVES:
                    for k in range(2):
                        load_w8(half + 1, k, k)
                    sp.wait_ge(part_done, TB * (half + 1))
                    for j in range(XP):
                        load_x(half + 1, j)
                for t in range(TB):
                    g = half * TB + t
                    sp.wait_ge(o_ready, g + 1)
                    sp.dma_start(out[g * P:(g + 1) * P, :], RES[t][:]).then_inc(o_out, 16)
            sp.wait_ge(o_out, 16 * HALVES * TB)

        @block.tensor
        def _(pe):
            def product(p, pair, x_parts=None, inside={}):
                tile = 2 * pair + p
                pe.wait_ge(w_lo, tile + 1)
                if not (isinstance(pair, int) and pair == 0):
                    pe.wait_ge(pj_free, tile - 1)
                for k in range(KD):
                    if x_parts is not None and k % (KD // XP) == 0:
                        pe.wait_ge(x_lo, x_parts + k // (KD // XP) + 1)
                    if k in inside:
                        inside[k]()
                    for n, (w, x) in enumerate(((WH, XH), (WH, XL), (WL, XH))):
                        for c in range(NC):
                            mm = nc.tensor.matmul(PJ[p][c][:], w[p][:, k, :], x[:, k, c * C:(c + 1) * C],
                                                  start=(k == 0 and n == 0), stop=(k == KD - 1 and n == 2))
                mm.then_inc(tile_done, 1)

            for h in range(HEADS):
                p = h % 2
                pe.wait_ge(w_lo, h + 1)
                if h >= 2:
                    pe.wait_ge(pj_free, h - 1)
                for k in range(KD):
                    if h == 0 and k % (KD // 2) == 0:
                        pe.wait_ge(m_lo, 2 * k // KD + 1)
                    for n, (w, x) in enumerate(((WH, MTH), (WH, MTL), (WL, MTH))):
                        mm = nc.tensor.matmul(PJ[p][0][:, 0:MEM], w[p][:, k, :], x[:, k, :],
                                              start=(k == 0 and n == 0), stop=(k == KD - 1 and n == 2))
                mm.then_inc(tile_done, 1)
            for h in range(HEADS):
                p = h % 2
                pe.wait_ge(w_lo, HEADS + h + 1)
                pe.wait_ge(pj_free, HEADS + h - 1)
                for m in range(MEM // P):
                    for k in range(KD):
                        for n, (x, w) in enumerate(((MTH, WH), (MTL, WH), (MTH, WL))):
                            mm = nc.tensor.matmul(PJ[p][0][:, m * P:(m + 1) * P], x[:, k, m * P:(m + 1) * P],
                                                  w[p][:, k, :], start=(k == 0 and n == 0),
                                                  stop=(k == KD - 1 and n == 2))
                mm.then_inc(tile_done, 1)

            pe.wait_ge(c_made, 5)

            def scores(half, h, s):
                s0 = half * HEADS * NS[0] + h * NS[half]
                c, b, a, first, end, diag = STEPS[half][s]
                if s == 0:
                    pe.wait_ge(pj_free, first_tile(half) + 4 * h + 2)
                if s < 4:
                    wait_if(pe, m_done, s0)
                    wait_if(pe, y_f, half * Y_HALF + h * NC)
                    if s == 3:
                        pe.wait_ge(pj_free, first_tile(half) + 4 * h + 3)
                else:
                    pe.wait_ge(m_done, s0 + s - 3)
                if s == 6:
                    pe.wait_ge(v_blk, 2 * (half * HEADS + h + 1))
                if half and b < half * TB:
                    pe.wait_ge(kv_back, 48 * (h + 1))
                q = slice(c * C + a, (c + 1) * C)
                for n, (kk, qq) in enumerate(((KH, QH), (KH, QL), (KL, QH))):
                    mm = nc.tensor.matmul(z_bank(s)[:, a:C], kk[:, b * P:(b + 1) * P], qq[:, q],
                                          start=n == 0, stop=n == 2)
                mm.then_inc(z_done, 1)

            def sums(half, h, r):
                s0 = half * HEADS * NS[0] + h * NS[half]
                c, b, a, first, end, diag = STEPS[half][r]
                pe.wait_ge(p_lo, s0 + r + 1)
                if first and c:
                    pe.wait_ge(m_done, s0 + 4)
                elif first:
                    wait_if(pe, arg_done, s0)
                nc.tensor.matmul(SUM[c][:, a:C], SUFFIX[:], PHI[r % 4][:, a:C], start=first, stop=False,
                                 skip_group_check=True)
                nc.tensor.matmul(SUM[c][:, a:C], SUFFIX[:], PLO[r % 4][:, a:C], start=False, stop=True,
                                 skip_group_check=True).then_inc(acc_done, 1)

            def carry(half, h, r):
                s0 = half * HEADS * NS[0] + h * NS[half]
                c, b, a, first, end, diag = STEPS[half][r]
                if not end:
                    pe.wait_ge(arg_done, s0 + r + 1)
                    nc.tensor.matmul(SUM[c][:, a:C], CARRY[:], PHI[r % 4][:, a:C], start=False, stop=False,
                                     skip_group_check=True)
                    nc.tensor.matmul(SUM[c][:, a:C], CARRY[:], PLO[r % 4][:, a:C], start=False, stop=True,
                                     skip_group_check=True)

            def attention(half, h):
                steps, ns = STEPS[half], NS[half]
                s0 = half * HEADS * NS[0] + h * ns

                def values(r):
                    c, b, a, first, end, diag = steps[r]
                    if r == 0:
                        pe.wait_ge(v_blk, 2 * (half * HEADS + h + 1))
                    pe.wait_ge(w_done, s0 + r + 1)
                    if first and c:
                        wait_if(pe, y_f, half * Y_HALF + h * NC)
                        pe.wait_ge(m_done, s0 + 3)
                    nc.tensor.matmul(OUT[c][:, a:C], V[:, b, :], W[r % 2][:, a:C], start=first, stop=end,
                                     skip_group_check=True).then_inc(pv_done, 1)

                carry(half, h, 0)
                sums(half, h, 1)
                scores(half, h, EARLY)
                pe.wait_ge(pj_free, first_tile(half) + 4 * h + 4)
                for i, turned in enumerate(TURNED):
                    for j in range(4):
                        mm = nc.tensor.transpose(turned[:, j * P:(j + 1) * P],
                                                 VT[:, (4 * i + j) * P:(4 * i + j + 1) * P], IDENT[:])
                    mm.then_inc(v_tr, 1)
                carry(half, h, 1)
                sums(half, h, 2)
                scores(half, h, EARLY + 1)
                values(0)
                values(1)
                carry(half, h, 2)
                for s in range(EARLY + 2, ns + USE):
                    if s - SUMS < ns:
                        sums(half, h, s - SUMS)
                    if s < ns:
                        scores(half, h, s)
                    values(s - USE)
                    if s - SUMS < ns:
                        carry(half, h, s - SUMS)

            def branch(half, n, i, p):
                pe.wait_ge(b_lo, (half * NB + n) * FT + 2 * i + p + 1)
                if p == 0:
                    pe.wait_ge(y_lo, half * Y_HALF + (n + 1) * KB * NC)
                for k in range(KB):
                    for m, (w, y) in enumerate(((BH, YH), (BH, YL), (BL, YH))):
                        for c in range(NC):
                            mm = nc.tensor.matmul(BR[p][c][:], w[p][:, k, :], y[:, k, c * C:(c + 1) * C],
                                                  start=(k == 0 and m == 0), stop=(k == KB - 1 and m == 2))
                mm.then_inc(branch_done, 1)

            def merge(half, n, inside={}):
                pair = first_tile(half, (M0, M1, M2, M3)[n]) // 2
                product(0, pair, inside=inside)
                product(1, pair)
                branch(half, n, 0, 0)
                branch(half, n, 0, 1)
                with pe.Fori(1, FT // 2) as i:
                    for p in range(2):
                        product(p, pair + i)
                        branch(half, n, i, p)

            for half in range(HALVES):
                def head(h, half=half):
                    pair = first_tile(half) // 2 + 2 * h
                    wait_if(pe, y_f, half * Y_HALF + h * NC - 1)
                    wait_if(pe, arg_done, half * HEADS * NS[0] + h * NS[half])
                    product(0, pair, x_parts=XP * half)
                    product(1, pair)
                    product(0, pair + 1)
                    for s in range(EARLY - 1):
                        scores(half, h, s)
                    product(1, pair + 1, inside={KD // 2: lambda: scores(half, h, EARLY - 1),
                                                 KD - 1: lambda: sums(half, h, 0)})
                    attention(half, h)

                each(pe, half == 0, HEADS, head)
                pe.wait_ge(y_f, half * Y_HALF + HEADS * NC - 1)
                pe.wait_ge(arg_done, HEADS * (NS[0] + half * NS[1]))
                merge(half, 0)
                for g in range(HEADS):
                    pair = first_tile(half, POOL0) // 2 + g
                    product(0, pair)
                    product(1, pair)
                    pe.wait_ge(pl_lo, half * HEADS + g + 1)
                    pe.wait_ge(pw_lo, half + 1)
                    pe.wait_ge(y_f, half * Y_HALF + (KB + g) * NC)
                    for n, (w, u) in enumerate(((WPH, PLH), (WPH, PLL), (WPL, PLH))):
                        for c in range(NC):
                            mm = nc.tensor.matmul(Z[c][:], w[:, g, :], u[:, c * C:(c + 1) * C], start=n == 0,
                                                  stop=n == 2)
                    mm.then_inc(mix_done, 1)
                merge(half, 1)
                def tile(g, half=half):
                    pair = first_tile(half, LRU0) // 2 + g
                    product(0, pair)
                    product(1, pair)
                    pe.wait_ge(xc_lo, half * HEADS + g + 1)
                    pe.wait_ge(gw_lo, half * HEADS + g + 1)
                    if isinstance(g, int):
                        wait_if(pe, l_act, 9 * half * HEADS)
                    else:
                        pe.wait_ge(l_act, 9 * (half * HEADS + g) - 5)
                    for r in range(2):
                        for n, (w, u) in enumerate(((WGH, XCH), (WGH, XCL), (WGL, XCH))):
                            for c in range(NC):
                                mm = nc.tensor.matmul(BR[r][c][:], w[:, r, :], u[:, c * C:(c + 1) * C],
                                                      start=n == 0, stop=n == 2)
                        mm.then_inc(gates_done, 1)

                each(pe, half == 0, HEADS, tile)
                merge(half, 2)
                def turned_use(hh):
                    pe.wait_ge(pt_done, 2 * NC * hh)
                    pe.wait_ge(vm_back, 16 * hh)
                    for c in range(NC):
                        for m in range(MEM // P):
                            mm = nc.tensor.matmul(BR[1][c][:], VM[:, m, :], PT[c][:, m, :],
                                                  start=m == 0, stop=m == MEM // P - 1)
                        mm.then_inc(xo_done, 1)

                def head(h, half=half):
                    hh = half * HEADS + h
                    pair = first_tile(half, XA0) // 2 + h
                    product(0, pair)
                    if not (isinstance(h, int) and h == 0):
                        turned_use(hh)
                    pe.wait_ge(km_back, 32 * (hh + 1))
                    pe.wait_ge(pj_free, 2 * pair + 1)
                    for c in range(NC):
                        if c:
                            pe.wait_ge(y_f, half * Y_HALF + (3 * KB + h) * NC)
                        for t in range(C // P):
                            q = slice(c * C + t * P, c * C + (t + 1) * P)
                            for n, (qq, kk) in enumerate(((QH, KM[0]), (QL, KM[0]), (QH, KM[1]))):
                                mm = nc.tensor.matmul(BR[c][t // 2][:, (t % 2) * MEM:(t % 2 + 1) * MEM], qq[:, q],
                                                      kk[:], start=n == 0, stop=n == 2)
                            if t % 2:
                                mm.then_inc(sc_done, 1)
                    product(1, pair)
                    for c in range(NC):
                        pe.wait_ge(nm_done, 4 * (NC * hh + c + 1))
                        for m in range(MEM // P):
                            for t in range(C // P):
                                mm = nc.tensor.transpose(BR[c][m][:, t * P:(t + 1) * P],
                                                         PR[c][:, t, m * P:(m + 1) * P], IDENT[:])
                            mm.then_inc(tr_done, 1)

                head(0)
                with pe.Fori(1, HEADS) as h:
                    head(h)
                merge(half, 3, {KD // 2: lambda: turned_use((half + 1) * HEADS)})
                tile0 = first_tile(half, WO0)
                for part in range(2):
                    pe.wait_ge(w_lo, tile0 + 4 * (part + 1))
                    wo_h, wo_l = WO[part]
                    for t in range(TB):
                        split = half * SPLITS + part * TB + t + 2
                        if part:
                            pe.wait_ge(part_free, half * TB + t + 1)
                        else:
                            pe.wait_ge(pj_free, tile0 if t >= 4 else tile0 - 1)
                        for k in range(KD):
                            if k == 0 and part == 0 and t == 0:
                                pe.wait_ge(mt_lo, split - 1)
                            if k == (PIECES[1][0] if part == 0 and t == 0 else 0):
                                pe.wait_ge(mt_lo, split)
                            for n, (m, w) in enumerate(((MH, wo_h), (MH, wo_l), (ML, wo_h))):
                                mm = nc.tensor.matmul(ROWS[t][:], m[t % 2][:, k, :], w[:, k, :],
                                                      start=(k == 0 and n == 0), stop=(k == KD - 1 and n == 2))
                        mm.then_inc(tile_done if part else part_done, 1)

        @block.scalar
        def _(act):
            def table(number):
                act.add_instruction(mybir.InstLoadActFuncSet(
                    name=nc.get_next_instruction_name(), engine=mybir.EngineType.Activation,
                    act_func_set_id=number))

            def split_w(pair, p):
                act.wait_ge(w_raw[p], 16 * pair + 16)
                if not (isinstance(pair, int) and pair == 0):
                    act.wait_ge(tile_done, 2 * pair + p - 1)
                nc.scalar.copy(WH[p][:], RAW[p][:]).then_inc(w_hi, 1)

            def split_out(half, k):
                tile0 = first_tile(half, WO0)
                act.wait_ge(w_raw[k % 2], 8 * (tile0 + k - k % 2) + 16)
                nc.scalar.copy(WO[k // 4][0][:, :, (k % 4) * P:(k % 4 + 1) * P], RAW[k % 2][:]).then_inc(w_hi, 1)

            def split_b(pair, p):
                act.wait_ge(b_raw[p], 16 * pair + 16)
                if not (isinstance(pair, int) and pair == 0):
                    act.wait_ge(branch_done, 2 * pair + p - 1)
                nc.scalar.copy(BH[p][:], BRAW[p][:]).then_inc(b_hi, 1)

            for i in range(2):
                k = slice(i * KD // 2, (i + 1) * KD // 2)
                act.wait_ge(m_in[i], 16)
                nc.scalar.copy(MTH[:, k], MRAW[:, k]).then_inc(m_hi, 1)
                if i == 0:
                    split_w(0, 0)
            split_w(0, 1)
            act.wait_ge(c_in, 32)
            for dst, col, n in ((IDENT, C_ID, P), (SUFFIX, C_SUF, P), (CARRY, C_CAR, P), (DIAG, C_DIAG, P)):
                nc.scalar.copy(dst[:], CRAW[:, col:col + n]).then_inc(c_made, 1)
            nc.scalar.copy(COUNT[:].rearrange("p a b -> p (a b)"), CRAW[:, C_CNT:C_ALL]).then_inc(c_made, 1)
            act.wait_ge(small, 2)
            table(SET_EXP_TANH)
            nc.scalar.activation(SM[:, KB:2 * KB], SM[:, 0:KB], ACT.Exp, scale=-1.0).then_inc(exp_l, 1)

            def split_x(half, j):
                k = slice(j * KD // XP, (j + 1) * KD // XP)
                act.wait_ge(x_in[j], 16 * (half + 1))
                if half:
                    act.wait_ge(tile_done, first_tile(half))
                nc.scalar.copy(XH[:, k, :], XRAW[:, k, :]).then_inc(x_hi, 1)

            for h in range(HEADS):
                act.wait_ge(tile_done, h + 1)
                nc.scalar.copy(KMA[0][:, h, :], PJ[h % 2][0][:, 0:MEM]).then_inc(mk_hi, 1)
                split_w(h // 2 + 1, h % 2)
            for h in range(HEADS):
                split_w((HEADS + h) // 2 + 1, h % 2)
                split_x(0, 2 * h)
                split_x(0, 2 * h + 1)
            act.wait_ge(pj_free, MEM_TILES)
            for h in range(HEADS):
                for i in range(2):
                    act.dma_start(km_keep[h, i], KMA[i][:, h, :].bitcast(F32)).then_inc(mk_kept, 16)
                act.dma_start(vm_keep[h], VMA[:, h].rearrange("p m d -> p (m d)")).then_inc(mk_kept, 16)

            def merge(half, n):
                tile0 = first_tile(half, (M0, M1, M2, M3)[n])
                g0 = (half * NB + n) * FT

                def pair(i, last):
                    for p in range(2):
                        f = 2 * i + p
                        if last and n == NB - 1 and p:
                            act.wait_ge(xo_done, (half + 1) * HEADS * NC)
                            act.wait_ge(y_lo, (half + 1) * Y_HALF)
                            for j in range(4):
                                split_out(half, j)
                        act.wait_ge(tile_done, tile0 + f + 1)
                        wait_if(act, merged, g0 + f - 1)
                        for c in range(NC):
                            nc.scalar.activation(GT[p][:, c * C:(c + 1) * C], PJ[p][c][:],
                                                 ACT.Sigmoid).then_inc(gate_sig, 1)
                        if not (last and n == NB - 1):
                            split_w(tile0 // 2 + i + 1, p)
                        if not last:
                            split_b(g0 // 2 + i + 1, p)

                table(SET_SIGMOID)
                split_b(g0 // 2, 0)
                split_b(g0 // 2, 1)
                if n == 0:
                    act.wait_ge(y_lo, half * Y_HALF + KB * NC)

                def pair_of_tiles(i, half=half):
                    pair(i, False)

                each(act, half == 0 and n == 0, FT // 2 - 1, pair_of_tiles)
                pair(FT // 2 - 1, True)

            def magnitude(half, h, s):
                s0 = half * HEADS * NS[0] + h * NS[half]
                a = STEPS[half][s][2]
                act.wait_ge(z_done, s0 + s + 1)
                wait_if(act, m_done, s0 + max(s - 2, 0))
                nc.scalar.activation(E[s % 3][:, a:C], z_bank(s)[:, a:C], ACT.Abs).then_inc(abs_done, 1)

            def exponential(half, h, s):
                s0 = half * HEADS * NS[0] + h * NS[half]
                e = E[s % 3][:, STEPS[half][s][2]:C]
                act.wait_ge(abs_done, s0 + s + 1)
                nc.scalar.activation(e, e, ACT.Exp, scale=-1.0).then_inc(exp_done, 1)

            def logarithm(half, h, s):
                s0 = half * HEADS * NS[0] + h * NS[half]
                e = E[s % 3][:, STEPS[half][s][2]:C]
                act.wait_ge(exp_done, s0 + s + 1)
                nc.scalar.activation(e, e, ACT.Ln, bias=1.0).then_inc(ln_done, 1)

            def attention(half, h):
                steps, ns = STEPS[half], NS[half]
                s0 = half * HEADS * NS[0] + h * ns
                hh = half * HEADS + h

                def weights(r):
                    a = steps[r][2]
                    act.wait_ge(arg_done, s0 + r + 1)
                    wait_if(act, pv_done, s0 + max(r - 1, 0))
                    nc.scalar.activation(W[r % 2][:, a:C], ARG[r % 4][:, a:C], ACT.Exp).then_inc(w_done, 1)

                for s in range(EARLY, ns + SUMS):
                    if EARLY < s <= ns:
                        logarithm(half, h, s - 1)
                    if s < ns:
                        magnitude(half, h, s)
                    if s == EARLY:
                        act.wait_ge(v_tr, 2 * (hh + 1))
                        weights(0)
                    weights(s - SUMS)
                    if s < ns:
                        exponential(half, h, s)
                    if s == 5:
                        act.wait_ge(w_raw[1], 8 * (first_tile(half) + 4 * h + 4) + 16)
                        act.wait_ge(tile_done, first_tile(half) + 4 * h + 4)
                    if 5 <= s < 7:
                        k = slice((s - 5) * KD // 2, (s - 4) * KD // 2)
                        mm = nc.scalar.copy(WH[1][:, k], RAW[1][:, k])
                        if s == 6:
                            mm.then_inc(w_hi, 1)
                    if s == 6 and half == 0:
                        act.wait_ge(v_blk, 2 * (hh + 1))
                        for i, kk in enumerate((KH, KL)):
                            act.dma_start(k_keep[bass.ds(h, 1), i].rearrange("o p n -> (o p) n"),
                                          kk[:, 0:T].bitcast(F32)).then_inc(kv_kept, 16)
                        act.dma_start(v_keep[bass.ds(h, 1)].rearrange("o p n -> (o p) n"),
                                      V[:, 0:TB, :].rearrange("p b d -> p (b d)")).then_inc(kv_kept, 16)

            for half in range(HALVES):
                def head(h, half=half):
                    hh = half * HEADS + h
                    s0 = half * HEADS * NS[0] + h * NS[half]
                    pair = first_tile(half) // 2 + 2 * h
                    wait_if(act, pv_done, s0)
                    wait_if(act, v_blk, 2 * hh)
                    wait_if(act, kv_kept, 48 * h if half == 0 else 48 * HEADS)
                    if half:
                        act.wait_ge(x_lo, XP * (half + 1))
                        for i, kk in enumerate((KH, KL)):
                            act.dma_start(kk[:, 0:T].bitcast(F32),
                                          k_keep[bass.ds(h, 1), i].rearrange("o p n -> (o p) n")).then_inc(kv_back, 16)
                        act.dma_start(V[:, 0:TB, :].rearrange("p b d -> p (b d)"),
                                      v_keep[bass.ds(h, 1)].rearrange("o p n -> (o p) n")).then_inc(kv_back, 16)
                    act.wait_ge(tile_done, 2 * pair + 1)
                    for c in range(NC):
                        nc.scalar.mul(QH[:, c * C:(c + 1) * C], PJ[0][c][:], SCALE).then_inc(q_hi, 1)
                    split_w(pair + 1, 0)
                    act.wait_ge(tile_done, 2 * pair + 2)
                    for c in range(NC):
                        nc.scalar.copy(KH[:, half * T + c * C:half * T + (c + 1) * C], PJ[1][c][:]).then_inc(k_hi, 1)
                    split_w(pair + 1, 1)
                    table(SET_SIGMOID)
                    act.wait_ge(tile_done, 2 * pair + 3)
                    wait_if(act, y_lo, half * Y_HALF + NC * h)
                    for c in range(NC):
                        nc.scalar.activation(SG[:, c * C:(c + 1) * C], PJ[0][c][:], ACT.Sigmoid).then_inc(sb_sig, 1)
                    table(SET_EXP_LN)
                    for s in range(EARLY + 1):
                        if s < EARLY:
                            magnitude(half, h, s)
                        if s:
                            logarithm(half, h, s - 1)
                        if s < EARLY:
                            exponential(half, h, s)
                    split_w(pair + 2, 0)
                    attention(half, h)

                each(act, half == 0, HEADS, head)
                act.wait_ge(kv_kept, 48 * HEADS)
                act.wait_ge(mk_kept, 48 * HEADS)
                merge(half, 0)
                act.dma_start(WPR[:].rearrange("p g n -> p (g n)"), wpool).then_inc(pw_in, 16)
                act.wait_ge(pw_in, 16 * (half + 1))
                nc.scalar.copy(WPH[:], WPR[:]).then_inc(pw_hi, 1)
                for g in range(HEADS):
                    gg = half * HEADS + g
                    pair = first_tile(half, POOL0) // 2 + g
                    split_w(pair + 1, 0)
                    act.wait_ge(pl_f, gg + 1)
                    wait_if(act, mix_done, gg)
                    nc.scalar.copy(PLH[:], PS[POOL_OUT[g]][:, HALO:]).then_inc(pl_hi, 1)
                    act.wait_ge(tile_done, 2 * pair + 2)
                    act.wait_ge(y_lo, half * Y_HALF + (KB + g) * NC)
                    for c in range(NC):
                        nc.scalar.activation(PG[:, c * C:(c + 1) * C], PJ[1][c][:], ACT.Sigmoid).then_inc(p_sig, 1)
                    split_w(pair + 1, 1)
                merge(half, 1)
                for g in range(HEADS):
                    gg = half * HEADS + g
                    pair = first_tile(half, LRU0) // 2 + g
                    act.wait_ge(branch_done, (half * NB + 2) * FT)
                    wait_if(act, gates_done, 2 * gg)
                    wait_if(act, gw_lo, gg)
                    act.dma_start(WGR[:].rearrange("p r n -> p (r n)"), wgate[g]).then_inc(gw_in, 16)
                    split_w(pair + 1, 0)
                    act.wait_ge(gw_in, 16 * gg + 16)
                    nc.scalar.copy(WGH[:], WGR[:]).then_inc(gw_hi, 1)
                    act.wait_ge(xc_f, gg + 1)
                    nc.scalar.copy(XCH[:], XC[g % 2][:]).then_inc(xc_hi, 1)
                    split_w(pair + 1, 1)
                    table(SET_SIGMOID)
                    act.wait_ge(y_f, half * Y_HALF + (2 * KB + g) * NC)
                    for r, dst in enumerate((LR, LI)):
                        act.wait_ge(gates_done, 2 * gg + r + 1)
                        for c in range(NC):
                            nc.scalar.activation(dst[:, c * C:(c + 1) * C], BR[r][c][:], ACT.Sigmoid,
                                                 bias=GP[:, P_BR + r:P_BR + r + 1]).then_inc(l_act, 1)
                    act.wait_ge(y_lo, half * Y_HALF + (2 * KB + g) * NC)
                    for c in range(NC):
                        nc.scalar.activation(LG[:, c * C:(c + 1) * C], PJ[1][c][:], ACT.Sigmoid).then_inc(l_act, 1)
                    table(SET_EXP_TANH)
                    act.wait_ge(l_act, 9 * gg + 4)
                    nc.scalar.activation(LA[:], LR[:], ACT.Exp, scale=GP[:, P_NSP:P_NSP + 1]).then_inc(l_act, 1)
                    nc.scalar.activation(LT[:], LR[:], ACT.Tanh, scale=GP[:, P_NSP:P_NSP + 1]).then_inc(l_act, 1)
                    table(SET_SQRT)
                    act.wait_ge(l_var, gg + 1)
                    nc.scalar.activation(LR[:], LR[:], ACT.Sqrt, scale=-ROOT_UP).then_inc(l_act, 1)
                merge(half, 2)
                def head(h, half=half):
                    hh = half * HEADS + h
                    pair = first_tile(half, XA0) // 2 + h
                    act.wait_ge(y_lo, half * Y_HALF + 3 * KB * NC)
                    wait_if(act, sc_done, 2 * NC * hh)
                    for i in range(2):
                        act.dma_start(KM[i][:].bitcast(F32), km_keep[bass.ds(h, 1), i].rearrange("o p n -> (o p) n")
                                      ).then_inc(km_back, 16)
                    act.wait_ge(tile_done, 2 * pair + 1)
                    for c in range(NC):
                        nc.scalar.mul(QH[:, c * C:(c + 1) * C], PJ[0][c][:], SCALE).then_inc(xq_hi, 1)
                    split_w(pair + 1, 0)
                    wait_if(act, xo_done, NC * hh)
                    act.dma_start(VM[:].rearrange("p m d -> p (m d)"),
                                  vm_keep[bass.ds(h, 1)].rearrange("o p n -> (o p) n")).then_inc(vm_back, 16)
                    table(SET_EXP_TANH)
                    wait_if(act, tr_done, 2 * NC * hh)
                    for c in range(NC):
                        act.wait_ge(mx_done, NC * hh + c + 1)
                        for t in range(C // P):
                            k = 16 * c + t
                            nc.scalar.activation(PR[c][:, t, :], BR[c][t // 2][:, (t % 2) * MEM:(t % 2 + 1) * MEM],
                                                 ACT.Exp, bias=SM[:, k + 4:k + 5],
                                                 accum_out=SM[:, k + 8:k + 9]).then_inc(ex_done, 1)
                    table(SET_SIGMOID)
                    act.wait_ge(tile_done, 2 * pair + 2)
                    act.wait_ge(y_lo, half * Y_HALF + (3 * KB + h) * NC)
                    for c in range(NC):
                        nc.scalar.activation(AG[:, c * C:(c + 1) * C], PJ[1][c][:], ACT.Sigmoid).then_inc(x_sig, 1)
                    split_w(pair + 1, 1)

                each(act, half == 0, HEADS, head)
                merge(half, 3)
                tile0 = first_tile(half, WO0)
                act.wait_ge(tile_done, tile0)
                table(SET_SQRT)
                for s in range(2 * TB):
                    part, t = s // TB, s % TB
                    if s == 0:
                        for k, end in PIECES:
                            act.wait_ge(merged, (half * NB + NB - 1) * FT + end)
                            nc.scalar.copy(MH[0][:, k:end, :], MERGED[:, k:end, 0:P]).then_inc(mt_hi, 1)
                    else:
                        wait_if(act, part_done, half * TB + min(s - 1, TB))
                        act.wait_ge(tile_done, tile0 + max(s - 1 - TB, 0))
                        nc.scalar.copy(MH[t % 2][:], MERGED[:, :, t * P:(t + 1) * P]).then_inc(mt_hi, 1)
                    if 1 <= s <= 4:
                        split_out(half, 3 + s)
                    if half + 1 < HALVES and s == TB + 3:
                        for p in range(2):
                            act.wait_ge(w_raw[p], 8 * first_tile(half + 1) + 16)
                            nc.scalar.copy(WH[p][:], RAW[p][:]).then_inc(w_hi, 1)
                    if s > TB:
                        g = half * TB + t - 1
                        act.wait_ge(var_done, g + 1)
                        nc.scalar.activation(SM2[:, 16:17], SM2[:, 13:14], ACT.Sqrt).then_inc(std_done, 1)
                if half + 1 < HALVES:
                    for j in range(XP):
                        split_x(half + 1, j)
                act.wait_ge(var_done, (half + 1) * TB)
                nc.scalar.activation(SM2[:, 16:17], SM2[:, 13:14], ACT.Sqrt).then_inc(std_done, 1)

        @block.vector
        def _(dve):
            chain = [0]

            def link(ins):
                chain[0] += 1
                ins.then_inc(small, 1)
                dve.wait_ge(small, chain[0])

            V_ = nc.vector

            def copy(dst, src):
                return V_.tensor_scalar(dst, src, 1.0, None, ALU.mult)

            for i in range(2):
                k = slice(i * KD // 2, (i + 1) * KD // 2)
                dve.wait_ge(m_hi, i + 1)
                V_.tensor_tensor(MTL[:, k], MRAW[:, k], MTH[:, k].bitcast(F32), ALU.subtract).then_inc(m_lo, 1)
            dve.wait_ge(c_in, 32)
            L = PRM[:, :, P_NSP]
            link(V_.tensor_scalar(SM[:, KB:2 * KB], L, -1.0, None, ALU.mult))
            link(V_.tensor_tensor(SM[:, 0:KB], SM[:, KB:2 * KB], L, ALU.max))
            dve.wait_ge(exp_l, 1)
            e, t, r, u, acc = (SM2[:, KB * i:KB * (i + 1)] for i in range(5))
            link(V_.tensor_copy(e, SM[:, KB:2 * KB]))
            link(V_.tensor_scalar(t, e, 2.0, None, ALU.add))
            link(V_.reciprocal(r, t))
            link(V_.tensor_tensor(t, e, r, ALU.mult))
            link(V_.tensor_tensor(u, t, t, ALU.mult))
            link(V_.memset(acc, 1.0 / 19.0))
            for k in range(17, 0, -2):
                link(V_.tensor_tensor(acc, acc, u, ALU.mult))
                link(V_.tensor_scalar(acc, acc, 1.0 / k, None, ALU.add))
            link(V_.tensor_tensor(acc, acc, t, ALU.mult))
            link(V_.tensor_scalar(acc, acc, -2.0 * LRU_C, None, ALU.mult))
            link(V_.tensor_scalar(e, L, 0.0, LRU_C, ALU.min, ALU.mult))
            link(V_.tensor_tensor(PRM[:, :, P_NSP], acc, e, ALU.add))
            link(V_.memset(HSTATE[:], 0.0))
            link(V_.memset(LHALO[:], 0.0))
            link(V_.memset(PHALO[:], 0.0))

            def rest_x(half, j):
                k = slice(j * KD // XP, (j + 1) * KD // XP)
                dve.wait_ge(x_hi, XP * half + j + 1)
                V_.tensor_tensor(XL[:, k, :], XRAW[:, k, :], XH[:, k, :].bitcast(F32), ALU.subtract).then_inc(x_lo, 1)

            for h in range(HEADS):
                dve.wait_ge(mk_hi, h + 1)
                V_.tensor_tensor(KMA[1][:, h, :], PJ[h % 2][0][:, 0:MEM], KMA[0][:, h, :].bitcast(F32),
                                 ALU.subtract).then_inc(pj_free, 1)
            for h in range(HEADS):
                dve.wait_ge(tile_done, HEADS + h + 1)
                V_.tensor_copy(VMA[:, h].rearrange("p m d -> p (m d)"), PJ[h % 2][0][:, 0:MEM]).then_inc(pj_free, 1)
                rest_x(0, 2 * h)
                rest_x(0, 2 * h + 1)

            def merge(half, n):
                tile0 = first_tile(half, (M0, M1, M2, M3)[n])
                g0 = (half * NB + n) * FT

                def product(f, p):
                    dve.wait_ge(branch_done, g0 + f + 1)
                    dve.wait_ge(gate_sig, 2 * (g0 + f + 1))
                    for c in range(NC):
                        s = slice(c * C, (c + 1) * C)
                        mm = V_.tensor_tensor(GT[p][:, s], BR[p][c][:], GT[p][:, s], ALU.mult)
                    mm.then_inc(pj_free, 1)

                last = n == NB - 1
                with dve.Fori(0, FT // 2 - last) as i:
                    for p in range(2):
                        product(2 * i + p, p)
                if last:
                    product(FT - 2, 0)
                    for k in range(4):
                        rest_out(half, k)
                    rest_merged(half, 0, 0)
                    product(FT - 1, 1)
                    dve.wait_ge(merged, g0 + FT - 1)
                    dve.wait_ge(pj_free, tile0 + FT)
                    V_.tensor_tensor(MERGED[:, FT - 1, :], MERGED[:, FT - 1, :], GT[1][:], ALU.add
                                     ).then_inc(merged, 1)

            def rest_merged(half, s, piece):
                k, end = PIECES[piece] if s == 0 else (0, KD)
                dve.wait_ge(mt_hi, half * SPLITS + s + 1 + (piece if s == 0 else 1))
                wait_if(dve, mt_lo, half * SPLITS)
                V_.tensor_tensor(ML[s][:, k:end, :], MERGED[:, k:end, s * P:(s + 1) * P],
                                 MH[s][:, k:end, :].bitcast(F32), ALU.subtract).then_inc(mt_lo, 1)

            def rest_out(half, k):
                s = slice((k % 4) * P, (k % 4 + 1) * P)
                hi, lo = (w[:, :, s] for w in WO[k // 4])
                dve.wait_ge(w_lo, first_tile(half, WO0) + k)
                dve.wait_ge(w_hi, first_tile(half, WO0) + k + 1)
                V_.tensor_tensor(lo, RAW[k % 2][:], hi.bitcast(F32), ALU.subtract).then_inc(w_lo, 1)

            def keep_y(half, n, h, c, src):
                dve.wait_ge(y_f, half * Y_HALF + (n * KB + h) * NC + c + 1)
                s = slice(c * C, (c + 1) * C)
                dst = YH[:, h, s] if isinstance(h, int) else YH[:, bass.ds(h, 1), s].rearrange("p o n -> p (o n)")
                copy(dst, src).then_inc(y_hi, 1)

            def argument(half, h, r):
                s0 = half * HEADS * NS[0] + h * NS[half]
                c, b, a, first, end, diag = STEPS[half][r]
                dve.wait_ge(acc_done, s0 + r + 1)
                dve.wait_ge(m_done, s0 + r + 1)
                if diag:
                    dve.wait_ge(m_masked, (half * HEADS + h) * ND + sum(step[5] for step in STEPS[half][:r + 1]))
                g = ARG[r % 4][:, a:C]
                V_.scalar_tensor_tensor(g, SUM[c][:, a:C], -1.0, g, ALU.mult, ALU.add).then_inc(arg_done, 1)

            def softplus(half, h, s):
                s0 = half * HEADS * NS[0] + h * NS[half]
                masked = (half * HEADS + h) * ND + sum(step[5] for step in STEPS[half][:s + 1])
                c, b, a, first, end, diag = STEPS[half][s]
                dve.wait_ge(ln_done, s0 + s + 1)
                wait_if(dve, p_lo, s0 + max(s - 1, 0))
                wait_if(dve, w_done, s0 + max(s - 3, 0))
                z, e = z_bank(s)[:, a:C], E[s % 3][:, a:C]
                V_.scalar_tensor_tensor(PF[s % 2][:, a:C], z, 0.0, e, ALU.max, ALU.add).then_inc(p_done, 1)
                V_.scalar_tensor_tensor(ARG[s % 4][:, a:C], z, 0.0, e, ALU.min, ALU.subtract).then_inc(m_done, 1)
                dve.wait_ge(p_done, s0 + s + 1)
                if diag:
                    m = PF[s % 2][:, a:a + P]
                    V_.tensor_tensor(m, m, DIAG[:], ALU.mult).then_inc(p_masked, 1)
                    dve.wait_ge(p_masked, masked)
                wait_if(dve, acc_done, s0 + max(s - 3, 0))
                V_.tensor_copy(PHI[s % 4][:, a:C], PF[s % 2][:, a:C]).then_inc(p_hi, 1)

            def attention(half, h):
                steps, ns = STEPS[half], NS[half]
                s0 = half * HEADS * NS[0] + h * ns
                hh = half * HEADS + h

                def output(c):
                    dve.wait_ge(pv_done, s0 + ENDS[half][c])
                    g = SG[:, c * C:(c + 1) * C]
                    V_.tensor_tensor(g, OUT[c][:], g, ALU.mult).then_inc(y_f, 1)
                    keep_y(half, 0, h, c, g)

                for i, turned in enumerate(TURNED):
                    dve.wait_ge(v_tr, 2 * hh + i + 1)
                    b = half * TB + 4 * i
                    V_.tensor_copy(V[:, b:b + 4, :].rearrange("p b d -> p (b d)"), turned[:]).then_inc(v_blk, 1)
                for s in range(EARLY, ns + SUMS):
                    if EARLY < s:
                        argument(half, h, s - SUMS)
                    if EARLY < s <= ns:
                        softplus(half, h, s - 1)
                for c in range(NC):
                    output(c)

            for half in range(HALVES):
                if half:
                    dve.wait_ge(o_ready, TB * half)
                    for j in range(XP - 2, XP):
                        rest_x(half, j)
                    dve.wait_ge(o_out, 16 * TB * half)

                def head(h, half=half):
                    hh = half * HEADS + h
                    s0 = half * HEADS * NS[0] + h * NS[half]
                    pair = first_tile(half) // 2 + 2 * h
                    dve.wait_ge(mk_kept, 48 * HEADS)
                    for c in range(NC):
                        s = slice(c * C, (c + 1) * C)
                        dve.wait_ge(q_hi, NC * hh + c + 1)
                        mm = V_.scalar_tensor_tensor(QL[:, s], PJ[0][c][:], SCALE, QH[:, s].bitcast(F32),
                                                     ALU.mult, ALU.subtract)
                    mm.then_inc(pj_free, 1)
                    for c in range(NC):
                        s = slice(half * T + c * C, half * T + (c + 1) * C)
                        dve.wait_ge(k_hi, NC * hh + c + 1)
                        mm = V_.tensor_tensor(KL[:, s], PJ[1][c][:], KH[:, s].bitcast(F32), ALU.subtract)
                    mm.then_inc(pj_free, 1)
                    for c in range(NC):
                        dve.wait_ge(sb_sig, NC * hh + c + 1)
                        g = SG[:, c * C:(c + 1) * C]
                        mm = V_.tensor_tensor(g, PJ[0][c][:], g, ALU.mult)
                    mm.then_inc(pj_free, 1)
                    V_.tensor_scalar(NEVER[:], DIAG[:], -1.0, 1e30, ALU.add, ALU.mult).then_inc(never_made, 1)
                    for s in range(EARLY):
                        softplus(half, h, s)
                    argument(half, h, 0)
                    dve.wait_ge(tile_done, 2 * pair + 4)
                    wait_if(dve, pv_done, s0)
                    V_.tensor_copy(VT[:, 0:C], PJ[1][0][:])
                    V_.tensor_copy(VT[:, C:T], PJ[1][1][:]).then_inc(pj_free, 1)
                    argument(half, h, 1)
                    attention(half, h)

                each(dve, half == 0, HEADS, head)
                merge(half, 0)
                for g in range(HEADS):
                    gg = half * HEADS + g
                    pair = first_tile(half, POOL0) // 2 + g
                    if half:
                        link(V_.tensor_copy(PU[:, 0:HALO], PHALO[:, g, :]))
                    else:
                        link(V_.memset(PU[:, 0:HALO], 0.0))
                    dve.wait_ge(tile_done, 2 * pair + 1)
                    for c in range(NC):
                        mm = V_.tensor_copy(PU[:, HALO + c * C:HALO + (c + 1) * C], PJ[0][c][:])
                    mm.then_inc(pj_free, 1)
                    dve.wait_ge(pj_free, 2 * pair + 1)
                    if half == 0:
                        link(V_.tensor_copy(PHALO[:, g, :], PU[:, T:]))
                    wait_if(dve, pl_lo, gg)
                    cur, lo = PU, 0
                    for m in range(g + 1):
                        nxt, sh = PS[m % 2], 1 << m
                        lo += sh
                        link(V_.tensor_tensor(nxt[:, lo:], cur[:, lo:], cur[:, lo - sh:HALO + T - sh], ALU.add))
                        cur = nxt
                    dst = PS[POOL_OUT[g]]
                    if half == 0:
                        link(V_.tensor_tensor(SM2[:, 0:HALO], cur[:, HALO:2 * HALO], COUNT[:, g, :], ALU.mult))
                        link(V_.tensor_tensor(dst[:, HALO:2 * HALO], SM2[:, 0:HALO], PU[:, HALO:2 * HALO],
                                              ALU.subtract))
                    a = 2 * HALO if half == 0 else HALO
                    V_.scalar_tensor_tensor(dst[:, a:], cur[:, a:], 1.0 / WINDOWS[g], PU[:, a:], ALU.mult,
                                            ALU.subtract).then_inc(pl_f, 1)
                    for c in range(NC):
                        dve.wait_ge(p_sig, NC * gg + c + 1)
                        q = PG[:, c * C:(c + 1) * C]
                        mm = V_.tensor_tensor(q, PJ[1][c][:], q, ALU.mult)
                    mm.then_inc(pj_free, 1)
                    dve.wait_ge(mix_done, gg + 1)
                    dve.wait_ge(pj_free, 2 * pair + 2)
                    for c in range(NC):
                        q = PG[:, c * C:(c + 1) * C]
                        V_.scalar_tensor_tensor(q, Z[c][:], PRM[:, g, P_SCALE:P_SCALE + 1], q, ALU.mult, ALU.mult
                                                ).then_inc(y_f, 1)
                        keep_y(half, 1, g, c, q)
                merge(half, 1)
                dve.wait_ge(merged, (half * NB + 2) * FT)
                for g in range(HEADS + 1):
                    gg = half * HEADS + g
                    pair = first_tile(half, LRU0) // 2 + g
                    if g < HEADS:
                        xc = XC[g % 2]
                        link(V_.tensor_copy(GP[:], PRM[:, g, :]))
                        link(V_.tensor_copy(LU[:, 0:4], LHALO[:, g, :]))
                        dve.wait_ge(tile_done, 2 * pair + 1)
                        for c in range(NC):
                            mm = V_.tensor_copy(LU[:, 4 + c * C:4 + (c + 1) * C], PJ[0][c][:])
                        mm.then_inc(pj_free, 1)
                        dve.wait_ge(pj_free, 2 * pair + 1)
                        link(V_.tensor_copy(LHALO[:, g, :], LU[:, T:T + 4]))
                        link(V_.tensor_scalar(xc[:], LU[:, 1:1 + T], GP[:, 0:1], GP[:, P_CB:P_CB + 1], ALU.mult,
                                              ALU.add))
                        for j in range(1, TAPS):
                            mm = V_.scalar_tensor_tensor(xc[:], LU[:, 1 + j:1 + j + T], GP[:, j:j + 1], xc[:],
                                                         ALU.mult, ALU.add)
                            if j < TAPS - 1:
                                link(mm)
                        mm.then_inc(xc_f, 1)
                    if g:
                        dve.wait_ge(l_act, 9 * gg)
                        link(V_.scalar_tensor_tensor(LR[:], LR[:], ROOT_DOWN, LI[:], ALU.mult, ALU.mult))
                    if g < HEADS:
                        dve.wait_ge(xc_hi, gg + 1)
                        V_.tensor_tensor(XCL[:], xc[:], XCH[:].bitcast(F32), ALU.subtract).then_inc(xc_lo, 1)
                    if g:
                        link(V_.tensor_tensor(LR[:], LR[:], XC[(g - 1) % 2][:], ALU.mult))
                        link(V_.tensor_copy(SM2[:, 0:1], HSTATE[:, g - 1:g]))
                        link(V_.tensor_tensor_scan(LT[:], LA[:], LR[:], SM2[:, 0:1], ALU.mult, ALU.add))
                        link(V_.tensor_copy(HSTATE[:, g - 1:g], LT[:, T - 1:T]))
                        dve.wait_ge(pj_free, 2 * pair)
                        for c in range(NC):
                            s = slice(c * C, (c + 1) * C)
                            V_.tensor_tensor(LG[:, s], LT[:, s], LG[:, s], ALU.mult).then_inc(y_f, 1)
                            keep_y(half, 2, g - 1, c, LG[:, s])
                    if g < HEADS:
                        for c in range(NC):
                            dve.wait_ge(l_act, 9 * gg + 5 + c)
                            q = LG[:, c * C:(c + 1) * C]
                            mm = V_.tensor_tensor(q, PJ[1][c][:], q, ALU.mult)
                        mm.then_inc(pj_free, 1)
                        dve.wait_ge(l_act, 9 * gg + 8)
                        link(V_.tensor_tensor(LR[:], LA[:], LA[:], ALU.mult))
                        V_.scalar_tensor_tensor(LR[:], LR[:], 1.0, LT[:], ALU.add, ALU.mult).then_inc(l_var, 1)
                merge(half, 2)
                NX = 6

                def x_output(h, half=half):
                    hh = half * HEADS + h
                    dve.wait_ge(pj_free, first_tile(half, XA0) + 2 * h + 2)
                    for c in range(NC):
                        dve.wait_ge(xo_done, NC * hh + c + 1)
                        q = AG[:, c * C:(c + 1) * C]
                        V_.tensor_tensor(q, BR[1][c][:], q, ALU.mult).then_inc(y_f, 1)
                    for c in range(NC):
                        keep_y(half, 3, h, c, AG[:, c * C:(c + 1) * C])

                def head(h, half=half):
                    hh = half * HEADS + h
                    pair = first_tile(half, XA0) // 2 + h
                    for c in range(NC):
                        s = slice(c * C, (c + 1) * C)
                        dve.wait_ge(xq_hi, NC * hh + c + 1)
                        mm = V_.scalar_tensor_tensor(QL[:, s], PJ[0][c][:], SCALE, QH[:, s].bitcast(F32),
                                                     ALU.mult, ALU.subtract)
                    mm.then_inc(pj_free, 1)
                    if not (isinstance(h, int) and h == 0):
                        x_output(h - 1)
                    wait_if(dve, ex_done, 4 * NC * hh)
                    for c in range(NC):
                        m = 16 * c
                        for i in range(2):
                            dve.wait_ge(sc_done, 2 * (NC * hh + c) + i + 1)
                            V_.reduce_max(SM[:, m + 2 * i:m + 2 * i + 2],
                                          BR[c][i][:].rearrange("p (t m) -> p t m", t=2), AX_X).then_inc(xm_step, 1)
                        dve.wait_ge(xm_step, NX * hh + 2 * c + 2)
                        V_.tensor_scalar(SM[:, m + 4:m + 8], SM[:, m:m + 4], -1.0, None, ALU.mult).then_inc(mx_done, 1)
                    for c in range(NC):
                        m = 16 * c
                        dve.wait_ge(ex_done, 4 * (NC * hh + c + 1))
                        V_.reciprocal(SM[:, m + 12:m + 16], SM[:, m + 8:m + 12]).then_inc(xm_step, 1)
                        dve.wait_ge(xm_step, NX * hh + 2 * NC + c + 1)
                        for t in range(C // P):
                            V_.tensor_scalar(PR[c][:, t, :], PR[c][:, t, :], SM[:, m + 12 + t:m + 13 + t], None,
                                             ALU.mult).then_inc(nm_done, 1)
                    for c in range(NC):
                        dve.wait_ge(x_sig, NC * hh + c + 1)
                        q = AG[:, c * C:(c + 1) * C]
                        mm = V_.tensor_tensor(q, PJ[1][c][:], q, ALU.mult)
                    mm.then_inc(pj_free, 1)
                    for c in range(NC):
                        for m in range(MEM // P):
                            dve.wait_ge(tr_done, 2 * (NC * hh + c) + m + 1)
                            V_.tensor_copy(PT[c][:, m, :], BR[c][m][:]).then_inc(pt_done, 1)

                head(0)
                with dve.Fori(1, HEADS) as h:
                    head(h)
                x_output(HEADS - 1)
                merge(half, 3)
                tile0 = first_tile(half, WO0)
                rest_merged(half, 0, 1)
                rest_merged(half, 1, 0)
                for part in range(2):
                    s = slice(part * C, (part + 1) * C)
                    for t in range(TB):
                        g = half * TB + t
                        if part:
                            dve.wait_ge(tile_done, tile0 + t + 1)
                        else:
                            dve.wait_ge(part_done, g + 1)
                            dve.wait_ge(xr_in[t], 16 * (half + 1))
                        V_.scalar_tensor_tensor(RES[t][:, s], RES[t][:, s], ALPHA, ROWS[t][:], ALU.mult, ALU.add
                                                ).then_inc(pj_free if part else part_free, 1)
                        if part == 0:
                            dve.wait_ge(part_free, g + 1)
                            V_.bn_stats(STATS[:, t, 0:6], RES[t][:, s]).then_inc(stat_done, 1)
                            if t < 4:
                                rest_out(half, 4 + t)
                            continue
                        if t == TB - 1 and half + 1 < HALVES:
                            for j in range(XP - 2):
                                rest_x(half + 1, j)
                        dve.wait_ge(pj_free, tile0 + t + 1)
                        link(V_.bn_stats(STATS[:, t, 6:12], RES[t][:, s]))
                        dve.wait_ge(stat_done, g + 1)
                        link(V_.bn_aggr(SM2[:, 12:14], STATS[:, t, :].rearrange("p (c k) -> p c k", c=2)))
                        wait_if(dve, std_done, g)
                        V_.tensor_scalar(SM2[:, 13:14], SM2[:, 13:14], LN_EPS, None, ALU.add).then_inc(var_done, 1)
                        dve.wait_ge(std_done, g + 1)
                        link(V_.reciprocal(SM2[:, 17:18], SM2[:, 16:17]))
                        link(V_.tensor_scalar(RES[t][:], RES[t][:], SM2[:, 12:13], SM2[:, 17:18], ALU.subtract,
                                              ALU.mult))
                        dve.wait_ge(ln_in, 32 * (half + 1))
                        link(V_.tensor_tensor(RES[t][:], RES[t][:], LNG[:], ALU.mult))
                        V_.tensor_tensor(RES[t][:], RES[t][:], LNB[:], ALU.add).then_inc(o_ready, 1)

        @block.gpsimd
        def _(pool):
            G_ = nc.gpsimd

            def rest_w(pair, p):
                pool.wait_ge(w_hi, 2 * pair + p + 1)
                G_.tensor_tensor(WL[p][:], RAW[p][:], WH[p][:].bitcast(F32), ALU.subtract).then_inc(w_lo, 1)

            def rest_b(pair, p):
                pool.wait_ge(b_hi, 2 * pair + p + 1)
                G_.tensor_tensor(BL[p][:], BRAW[p][:], BH[p][:].bitcast(F32), ALU.subtract).then_inc(b_lo, 1)

            def rest_y(half, n, h, c, src):
                pool.wait_ge(y_hi, half * Y_HALF + (n * KB + h) * NC + c + 1)
                s = slice(c * C, (c + 1) * C)
                if isinstance(h, int):
                    hi, lo = YH[:, h, s], YL[:, h, s]
                else:
                    hi, lo = (y[:, bass.ds(h, 1), s].rearrange("p o n -> p (o n)") for y in (YH, YL))
                G_.tensor_tensor(lo, src, hi.bitcast(F32), ALU.subtract).then_inc(y_lo, 1)

            def rest_merged(half, s):
                t = s % TB
                pool.wait_ge(mt_hi, half * SPLITS + s + 2)
                pool.wait_ge(mt_lo, half * SPLITS + s + 1)
                G_.tensor_tensor(ML[t % 2][:], MERGED[:, :, t * P:(t + 1) * P], MH[t % 2][:].bitcast(F32),
                                 ALU.subtract).then_inc(mt_lo, 1)

            for k in range(MEM_TILES + 2):
                rest_w(k // 2, k % 2)

            def merge(half, n):
                tile0 = first_tile(half, (M0, M1, M2, M3)[n])
                g0 = (half * NB + n) * FT

                def pair(i, last):
                    for p in range(2):
                        f = 2 * i + p
                        if not (last and n == NB - 1):
                            rest_w(tile0 // 2 + i + 1, p)
                        if not last:
                            rest_b(g0 // 2 + i + 1, p)
                        if last and n == NB - 1 and p:
                            continue
                        pool.wait_ge(pj_free, tile0 + f + 1)
                        wait_if(pool, merged, g0 + f)
                        d = MERGED[:, f, :] if isinstance(f, int) else \
                            MERGED[:, bass.ds(f, 1), :].rearrange("p o n -> p (o n)")
                        G_.tensor_tensor(d, d, GT[p][:], ALU.add).then_inc(merged, 1)

                rest_b(g0 // 2, 0)
                rest_b(g0 // 2, 1)
                if n == 0:
                    pool.wait_ge(pv_done, HEADS * (NS[0] + half * NS[1]))
                    G_.memset(MERGED[:], 0.0).then_inc(zeroed, 1)
                    pool.wait_ge(zeroed, half + 1)

                def pair_of_tiles(i, half=half):
                    pair(i, False)

                each(pool, half == 0 and n == 0, FT // 2 - 1, pair_of_tiles)
                pair(FT // 2 - 1, True)

            def rest_p(half, h, s):
                s0 = half * HEADS * NS[0] + h * NS[half]
                a = STEPS[half][s][2]
                if STEPS[half][s][5]:
                    pool.wait_ge(m_done, s0 + s + 1)
                    m = ARG[s % 4][:, a:a + P]
                    G_.tensor_tensor(m, m, NEVER[:], ALU.add).then_inc(m_masked, 1)
                pool.wait_ge(p_hi, s0 + s + 1)
                G_.tensor_tensor(PLO[s % 4][:, a:C], PF[s % 2][:, a:C], PHI[s % 4][:, a:C].bitcast(F32),
                                 ALU.subtract).then_inc(p_lo, 1)

            def attention(half, h):
                steps, ns = STEPS[half], NS[half]
                s0 = half * HEADS * NS[0] + h * ns
                for s in range(EARLY, ns + SUMS):
                    if EARLY < s <= ns:
                        rest_p(half, h, s - 1)
                    if s == 7:
                        pool.wait_ge(w_hi, first_tile(half) + 4 * h + 6)
                    if 7 <= s < 11:
                        k = slice((s - 7) * KD // 4, (s - 6) * KD // 4)
                        mm = G_.tensor_tensor(WL[1][:, k], RAW[1][:, k], WH[1][:, k].bitcast(F32), ALU.subtract)
                        if s == 10:
                            mm.then_inc(w_lo, 1)
                for c in range(NC):
                    rest_y(half, 0, h, c, SG[:, c * C:(c + 1) * C])

            for half in range(HALVES):
                def head(h, half=half):
                    pair = first_tile(half) // 2 + 2 * h
                    rest_w(pair + 1, 0)
                    rest_w(pair + 1, 1)
                    pool.wait_ge(never_made, half * HEADS + h + 1)
                    for s in range(EARLY):
                        rest_p(half, h, s)
                    rest_w(pair + 2, 0)
                    attention(half, h)

                each(pool, half == 0, HEADS, head)
                merge(half, 0)
                pool.wait_ge(pw_hi, half + 1)
                G_.tensor_tensor(WPL[:], WPR[:], WPH[:].bitcast(F32), ALU.subtract).then_inc(pw_lo, 1)
                for g in range(HEADS):
                    gg = half * HEADS + g
                    pair = first_tile(half, POOL0) // 2 + g
                    rest_w(pair + 1, 0)
                    pool.wait_ge(pl_hi, gg + 1)
                    G_.tensor_tensor(PLL[:], PS[POOL_OUT[g]][:, HALO:], PLH[:].bitcast(F32), ALU.subtract
                                     ).then_inc(pl_lo, 1)
                    rest_w(pair + 1, 1)
                    for c in range(NC):
                        rest_y(half, 1, g, c, PG[:, c * C:(c + 1) * C])
                merge(half, 1)
                for g in range(HEADS + 1):
                    gg = half * HEADS + g
                    pair = first_tile(half, LRU0) // 2 + g
                    if g < HEADS:
                        rest_w(pair + 1, 0)
                        pool.wait_ge(gw_hi, gg + 1)
                        G_.tensor_tensor(WGL[:], WGR[:], WGH[:].bitcast(F32), ALU.subtract).then_inc(gw_lo, 1)
                    if g:
                        for c in range(NC):
                            rest_y(half, 2, g - 1, c, LG[:, c * C:(c + 1) * C])
                    if g < HEADS:
                        rest_w(pair + 1, 1)
                merge(half, 2)

                def x_output(h, half=half):
                    for c in range(NC):
                        rest_y(half, 3, h, c, AG[:, c * C:(c + 1) * C])

                def head(h, half=half):
                    pair = first_tile(half, XA0) // 2 + h
                    rest_w(pair + 1, 0)
                    if not (isinstance(h, int) and h == 0):
                        x_output(h - 1)
                    rest_w(pair + 1, 1)

                head(0)
                with pool.Fori(1, HEADS) as h:
                    head(h)
                x_output(HEADS - 1)
                merge(half, 3)
                for s in range(2, 2 * TB):
                    rest_merged(half, s)
                    if half + 1 < HALVES and s == TB + 3:
                        rest_w(first_tile(half + 1) // 2, 0)
                        rest_w(first_tile(half + 1) // 2, 1)


def _tiles(np, w, rows, cols):
    return w.reshape(rows // P, P, cols // P, P).transpose(2, 1, 0, 3).reshape(cols // P, P, rows // P * P)


def kernel(**inputs):
    import numpy as np
    import concourse.bacc as bacc
    from concourse.bass_utils import run_bass_kernel_spmd

    a = {k: np.asarray(v) for k, v in inputs.items()}
    x = a["x"][0]
    w_in = _tiles(np, a["w_in"][0], D, a["w_in"].shape[2])
    order = [j * HEADS + h for h in range(HEADS) for j in (0, 1, 3, 2)]
    merge0 = 10 * HEADS
    order += [merge0 + f for f in range(FT)]
    for n in range(1, NB):
        order += [(4 + 2 * (n - 1) + j) * HEADS + h for h in range(HEADS) for j in range(2)]
        order += [merge0 + n * FT + f for f in range(FT)]
    w8 = np.concatenate([_tiles(np, a["w_mem_kv"][0], D, 2 * HEADS * P), w_in[order],
                         _tiles(np, a["w_out"][0], D, D)])
    w4 = np.concatenate([_tiles(np, a["w_branch"][0, n], KB * P, D) for n in range(NB)])
    xt = x.reshape(HALVES, T, KD, P).transpose(0, 3, 2, 1)
    memt = a["mem"][0].reshape(MEM, KD, P).transpose(2, 1, 0)
    wgate = np.zeros((KB, P, 2, P), np.float32)
    for r, name in enumerate(("w_rg", "w_ig")):
        for b in range(2):
            s = slice(64 * b, 64 * b + 64)
            wgate[:, s, r, s] = a[name][0][b::2]
    wpool = a["w_pool"][0].transpose(1, 0, 2).reshape(P, HEADS * P)
    cols = [a["conv_w"][0][j] for j in range(TAPS)]
    cols += [a[n][0] for n in ("conv_b", "b_rg", "b_ig", "lru_L", "pool_scale")]
    prm = np.stack(cols).reshape(P_ALL, KB, P).transpose(2, 1, 0).reshape(P, KB * P_ALL)
    cst = np.zeros((P, C_ALL), np.float32)
    i = np.arange(P)
    cst[:, C_ID:C_ID + P] = i[:, None] == i[None, :]
    cst[:, C_SUF:C_SUF + P] = i[:, None] > i[None, :]
    cst[:, C_CAR:C_CAR + P] = i[:, None] <= i[None, :]
    cst[:, C_DIAG:C_DIAG + P] = i[:, None] < i[None, :]
    for g, w in enumerate(WINDOWS):
        cst[:, C_CNT + g * HALO:C_CNT + (g + 1) * HALO] = 1.0 / np.minimum(np.arange(HALO) + 1, w)
    arrays = {"xt": xt, "xrow": x, "memt": memt, "w8": w8, "w4": w4, "wgate": wgate.reshape(KB, P, 2 * P),
              "wpool": wpool, "prm": prm, "cst": cst, "ln_g": a["ln_g"][0], "ln_b": a["ln_b"][0]}
    arrays = {k: np.ascontiguousarray(v) for k, v in arrays.items()}

    nc = bacc.Bacc("TRN2", target_bir_lowering=False, num_devices=1)
    args = [nc.dram_tensor(k, v.shape, F32, kind="ExternalInput").ap() for k, v in arrays.items()]
    out = nc.dram_tensor("out", (SEQ, D), F32, kind="ExternalOutput").ap()
    build(nc, *args, out)
    r = run_bass_kernel_spmd(nc, [arrays], core_ids=[0])
    return r.results[0]["out"].reshape(1, SEQ, D)
```
